# Optimizing a Trainium2 kernel written in Bass

```python
import jax, jax.numpy as jnp
from jax import lax
import numpy as np

D_MODEL = 1024
BATCH = 1
SEQ = 512
DEPTH = 1
DEC_BATCH = 1
DEC_SEQ = 1024
PAST_LEN = 128

GRID_W = 64
D_CONV = 1024
CONV_K = 31
N_HEADS = 16
HEAD_DIM = 64
D_ATTN = N_HEADS * HEAD_DIM
WIN_ROWS_MAX = 8
WIN_COLS = 16
Q_COL_BLOCK = 16
K_COL_BAND = Q_COL_BLOCK + WIN_COLS
N_COL_BLOCKS = GRID_W // Q_COL_BLOCK
D_IN = 3 * D_CONV + 4 * D_ATTN + 2 * D_MODEL
RMS_EPS = 1e-6
LN_EPS = 1e-5
NEG_INF = -1e30

kernel_name = "gated_conformer_conv_neighbourhood_attn_encoder"

def _rmsnorm(x, g):
    xf = x.astype(jnp.float32)
    y = xf * lax.rsqrt(jnp.mean(xf * xf, axis=-1, keepdims=True) + RMS_EPS)
    return (y * g.astype(jnp.float32)).astype(x.dtype)

def _layernorm(x, g, b):
    xf = x.astype(jnp.float32)
    mu = jnp.mean(xf, axis=-1, keepdims=True)
    var = jnp.mean(jnp.square(xf - mu), axis=-1, keepdims=True)
    y = (xf - mu) * lax.rsqrt(var + LN_EPS)
    return (y * g.astype(jnp.float32) + b.astype(jnp.float32)).astype(x.dtype)

def _col_tables():
    j = np.arange(N_COL_BLOCKS)
    band_start = np.clip(j * Q_COL_BLOCK - WIN_COLS // 2, 0, GRID_W - K_COL_BAND)
    key_col = band_start[:, None] + np.arange(K_COL_BAND)[None, :]
    q_col = j[:, None] * Q_COL_BLOCK + np.arange(Q_COL_BLOCK)[None, :]
    win_start = np.clip(q_col - WIN_COLS // 2, 0, GRID_W - WIN_COLS)
    kc = key_col[:, None, :]
    valid = (kc >= win_start[..., None]) & (kc < win_start[..., None] + WIN_COLS)
    col_idx = np.clip(kc - q_col[..., None], -(WIN_COLS - 1), WIN_COLS - 1) + WIN_COLS - 1
    return key_col, valid, col_idx

def _neighbourhood_attention(q, k, v, rpb):
    bsz, seq_len = q.shape[0], q.shape[1]
    rows = seq_len // GRID_W
    kh = min(WIN_ROWS_MAX, rows)
    grid = (bsz, rows, GRID_W, N_HEADS, HEAD_DIM)
    q, k, v = q.reshape(grid), k.reshape(grid), v.reshape(grid)
    key_col, valid, col_idx = _col_tables()
    valid_m = jnp.asarray(valid)[:, :, None, None, :]
    scale = HEAD_DIM ** -0.5

    def row_step(args):
        r, q_row = args
        rs = jnp.clip(r - kh // 2, 0, rows - kh)
        k_band = lax.dynamic_slice_in_dim(k, rs, kh, axis=1)[:, :, key_col]
        v_band = lax.dynamic_slice_in_dim(v, rs, kh, axis=1)[:, :, key_col]
        qb = q_row.reshape(bsz, N_COL_BLOCKS, Q_COL_BLOCK, N_HEADS, HEAD_DIM)
        s = jnp.einsum('bjqhd,bijkhd->bjqhik', qb, k_band,
                       preferred_element_type=jnp.float32) * scale
        row_idx = rs + jnp.arange(kh) - r + WIN_ROWS_MAX - 1
        rpb_r = rpb[:, row_idx, :].astype(jnp.float32)
        bias = rpb_r[:, :, col_idx].transpose(2, 3, 0, 1, 4)
        s = jnp.where(valid_m, s + bias, NEG_INF)
        p = jax.nn.softmax(s.reshape(s.shape[:4] + (kh * K_COL_BAND,)), axis=-1).reshape(s.shape)
        o = jnp.einsum('bjqhik,bijkhd->bjqhd', p.astype(v_band.dtype), v_band)
        return o.reshape(bsz, GRID_W, N_HEADS, HEAD_DIM)

    out = lax.map(row_step, (jnp.arange(rows), q.transpose(1, 0, 2, 3, 4)))
    return out.transpose(1, 0, 2, 3, 4).reshape(bsz, seq_len, D_ATTN)

def _conv_module(a_val, a_glu, dw_w, dw_b, ln_g, ln_b):
    u = a_val * jax.nn.sigmoid(a_glu)
    c = lax.conv_general_dilated(
        u, dw_w[:, None, :].astype(u.dtype), window_strides=(1,),
        padding=[(CONV_K // 2, CONV_K // 2)],
        dimension_numbers=('NWC', 'WIO', 'NWC'),
        feature_group_count=D_CONV) + dw_b
    return jax.nn.silu(_layernorm(c, ln_g, ln_b))

def _layer(x, norm_g, w_in, b_gate, dw_w, dw_b, ln_g, ln_b, w_pw_a, rpb, w_o_b, w_out):
    bsz, seq_len, _ = x.shape
    h = _rmsnorm(x, norm_g)
    proj = h @ w_in
    sizes = [D_CONV, D_CONV, D_CONV, D_ATTN, D_ATTN, D_ATTN, D_ATTN, 2 * D_MODEL]
    a_val, a_glu, z_a, q, k, v, z_b, g_logits = jnp.split(proj, np.cumsum(sizes)[:-1].tolist(), axis=-1)
    y_a = (_conv_module(a_val, a_glu, dw_w, dw_b, ln_g, ln_b) * jax.nn.silu(z_a)) @ w_pw_a
    hs = (bsz, seq_len, N_HEADS, HEAD_DIM)
    attn = _neighbourhood_attention(q.reshape(hs), k.reshape(hs), v.reshape(hs), rpb)
    y_b = (attn * jax.nn.silu(z_b)) @ w_o_b
    gates = jax.nn.sigmoid(g_logits + b_gate)
    g_a, g_b = gates[..., :D_MODEL], gates[..., D_MODEL:]
    merged = g_a * y_a + g_b * y_b
    return x + merged @ w_out

def _trunk(x, norm_g, w_in, b_gate, dw_w, dw_b, ln_g, ln_b, w_pw_a, rpb, w_o_b, w_out, final_g):
    for l in range(DEPTH):
        x = _layer(x, norm_g[l], w_in[l], b_gate[l], dw_w[l], dw_b[l], ln_g[l], ln_b[l],
                   w_pw_a[l], rpb[l], w_o_b[l], w_out[l])
    return _rmsnorm(x, final_g)

def setup_inputs(seed: int = 0) -> dict:
    key = jax.random.key(seed)
    ks = jax.random.split(key, 16)
    f32 = jnp.float32
    nrm = lambda k, shape, s: jax.random.normal(k, shape, f32) * s
    return {
        "x_prompt": nrm(ks[0], (BATCH, SEQ, D_MODEL), 1.0),
        "x_sample": nrm(ks[1], (DEC_BATCH, DEC_SEQ, D_MODEL), 1.0),
        "norm_g": 1.0 + nrm(ks[2], (DEPTH, D_MODEL), 0.02),
        "w_in": nrm(ks[3], (DEPTH, D_MODEL, D_IN), D_MODEL ** -0.5),
        "b_gate": nrm(ks[4], (DEPTH, 2 * D_MODEL), 0.01),
        "dw_w": nrm(ks[5], (DEPTH, CONV_K, D_CONV), CONV_K ** -0.5),
        "dw_b": nrm(ks[6], (DEPTH, D_CONV), 0.02),
        "ln_g": 1.0 + nrm(ks[7], (DEPTH, D_CONV), 0.02),
        "ln_b": nrm(ks[8], (DEPTH, D_CONV), 0.02),
        "w_pw_a": nrm(ks[9], (DEPTH, D_CONV, D_MODEL), D_CONV ** -0.5),
        "rpb": nrm(ks[10], (DEPTH, N_HEADS, 2 * WIN_ROWS_MAX - 1, 2 * WIN_COLS - 1), 0.1),
        "w_o_b": nrm(ks[11], (DEPTH, D_ATTN, D_MODEL), D_ATTN ** -0.5),
        "w_out": nrm(ks[12], (DEPTH, D_MODEL, D_MODEL), D_MODEL ** -0.5),
        "final_g": 1.0 + nrm(ks[13], (D_MODEL,), 0.02),
    }

def reference(x_prompt, x_sample, norm_g, w_in, b_gate, dw_w, dw_b, ln_g, ln_b, w_pw_a, rpb, w_o_b, w_out, final_g):
    y_prompt = _trunk(x_prompt, norm_g, w_in, b_gate, dw_w, dw_b, ln_g, ln_b, w_pw_a, rpb, w_o_b, w_out, final_g)
    y_sample = _trunk(x_sample, norm_g, w_in, b_gate, dw_w, dw_b, ln_g, ln_b, w_pw_a, rpb, w_o_b, w_out, final_g)
    return (y_prompt, y_sample)


_drawn_inputs = setup_inputs


def setup_inputs(seed=0):
    import zlib

    import numpy as np

    out = dict(_drawn_inputs(seed))
    spreads = {}
    factors = {'norm_g': 8.0,
     'b_gate': 42.54,
     'dw_b': 24.411,
     'ln_g': 39.284,
     'ln_b': 40.232,
     'rpb': 8.0,
     'final_g': 7.548}
    for name, (base, spread) in spreads.items():
        noise = np.random.default_rng([zlib.crc32(name.encode()), seed]).standard_normal(out[name].shape)
        drawn = base * np.exp(spread * noise) if base else spread * noise
        out[name] = __import__('jax').numpy.asarray(drawn.astype(out[name].dtype))
    for name, factor in factors.items():
        out[name] = (out[name] * factor).astype(out[name].dtype)
    return out
```

```python
from contextlib import ExitStack

import numpy as np

import concourse.bass as bass
from concourse import mybir
from concourse.alu_op_type import AluOpType as ALU

F32 = mybir.dt.float32
F32R = mybir.dt.float32r
BF16 = mybir.dt.bfloat16
ACT = mybir.ActivationFunctionType

P = 128
D = 1024
KT = D // P
PROMPT, SAMPLE = 512, 1024
TOK = PROMPT + SAMPLE
CH = 512
NCH = TOK // CH
NT = TOK // P
GRID = 64
HEADS, HD = 16, 64
PAIRS = HEADS // 2
TAPS = 31
PAD = TAPS // 2
ULEN = PAD + PROMPT + PAD + SAMPLE + PAD
CLEN = ULEN - 2 * PAD
QB = 16
BAND = 32
BAND_START = [0, 8, 24, 32]
JKIND = [0, 1, 1, 2]
SEG_ROWS = [8, 12, 12]
SEG_KEY0 = [0, 512, 512 + 4 * GRID]
SEG_RG = [0, 2, 3]
SEG_E0 = [4, 4, 0]
BLK = 24
KINDS = 9
KIND_OFF = [0, 256, 512, 768, 1152, 1536, 1920, 2304, 2688]
MASKLEN = 3072
RROWS, RCOLS = 23, 64
EROWS, ECOLS = 16, 48
NPAR = TAPS + 6
I_DWB, I_LNG, I_LNB, I_NG, I_BGA, I_BGB = range(TAPS, NPAR)

C_A, C_GLU, C_ZA, C_Q, C_K, C_V, C_ZB, C_GA, C_GB = (KT * n for n in range(9))

G_PRO = 2 * NT
G_UNIT = G_PRO + 4 * NCH
G_UNIT1 = G_UNIT + 6 * NCH
G_YB = G_UNIT1 + 24 * (PAIRS - 2) + 6 * NCH
G_YA = G_YB + 24
G_OUT = G_YA + 24
S_PRO = 8
S_UNIT = S_PRO + 4
S_UNIT1 = S_UNIT + 6
S_YB = S_UNIT1 + 8 * (PAIRS - 2) + 6
S_YA = S_YB + 8
S_OUT = S_YA + 8
S_END = S_OUT + 8
T_ZB, T_ZA, T_GA, T_GB, T_A, T_GLU, T_Q, T_K, T_GA2, T_GB2 = range(10)
FIRST_UNIT = (T_ZB, T_ZA, T_A, T_GLU, T_Q, T_K)
UNIT = (T_ZB, T_ZA, T_GA, T_GB, T_A, T_GLU, T_Q, T_K)
LAST_UNIT = (T_ZB, T_ZA, T_GA, T_GB, T_GA2, T_GB2)

RMS_EPS, LN_EPS = 1e-6, 1e-5
BIG = 1e30


EARLY = 11
EARLY0 = 19

def tiles_of(i):
    if isinstance(i, int):
        return FIRST_UNIT if i == 0 else LAST_UNIT
    return UNIT


def late_taps(i, slot):
    if isinstance(i, int) and i == 0:
        return range(EARLY0 + slot, min(EARLY0 + slot + 1, TAPS))
    n = TAPS - EARLY
    return range(EARLY + n * slot // BLK, EARLY + n * (slot + 1) // BLK)


def h_tiles(j):
    return range(3 * j, min(3 * j + 3, KT))


def piece_done(s):
    return G_PRO + 3 * (s - S_PRO) + 3


def build(nc, x_prompt, x_sample, norm_g, w_in, b_gate, dw_w, dw_b, ln_g, ln_b, w_pw_a, rpb,
          w_o_b, w_out, final_g, masks, y_prompt, y_sample):
    with ExitStack() as ctx:
        def sb(name, shape, dt=F32):
            return ctx.enter_context(nc.sbuf_tensor(name, shape, dt))

        def sem(name):
            return ctx.enter_context(nc.semaphore(name))

        def scratch(name, shape):
            return nc.dram_tensor(name, shape, F32, kind="Internal").ap()

        xs = sb("xs", [P, KT, 2, TOK], F32R)
        ws = sb("ws", [P, 4, 2, D], F32R)
        raw = sb("raw", [P, 2, D])
        ident = sb("ident", [P, P])
        par = sb("par", [P, KT, NPAR])
        small = sb("small", [P, 34])
        work = sb("work", [P, 17920])
        at = [0]

        def take(n):
            at[0] += n
            return work[:, at[0] - n:at[0]]

        qT = take(TOK)
        kT = take(TOK)
        vb = take(24 * P).rearrange("p (g j d) -> p g j d", g=6, j=4)
        tt = take(3 * 384).rearrange("p (s n) -> p s n", s=3)
        pt = take(2 * 384).rearrange("p (s n) -> p s n", s=2)
        bt = take(3 * 384).rearrange("p (s n) -> p s n", s=3)
        et = take(EROWS * ECOLS).rearrange("p (r c) -> p r c", r=EROWS)
        mask = take(MASKLEN // 2).bitcast(BF16)
        u = take(ULEN + 3)
        cv = take(CLEN + 1)
        tb = take(TOK)
        stage = take(3 * CH).rearrange("p (s n) -> p s n", s=3)
        cur = take(TAPS + 3)
        xt = work[:, 0:8 * D].rearrange("p (s t d) -> p s t d", s=2, t=4)
        junk = work[:, 8 * D:9 * D]
        msk32 = work[:, 11520:11520 + MASKLEN]
        prow = work[:, 14656:14656 + D]
        table = work[:, 0:RROWS * RCOLS]
        tbs = work[:, 0:7 * TOK].rearrange("p (k t) -> p k t", k=7)
        cs = work[:, 0:8 * TOK].rearrange("p (k t) -> p k t", k=8)
        lnA = work[:, 12288:12288 + TOK]
        lnB = work[:, 13824:13824 + TOK]
        tmp3 = work[:, 15360:15360 + TOK]
        diag = tmp3.rearrange("p (t n) -> p t n", n=P)
        gst = work[:, 16896:16896 + 2 * CH].rearrange("p (s n) -> p s n", s=2)
        mst = work[:, 15360:15360 + 2 * CH].rearrange("p (s n) -> p s n", s=2)
        res = work[:, 0:NT * CH].rearrange("p (t n) -> p t n", t=NT)
        fg = work[:, NT * CH:NT * CH + D]
        xre = work[:, 7168:7168 + 4 * CH].rearrange("p (s n) -> p s n", s=4)
        yst = work[:, 9216:9216 + 2 * D].rearrange("p (s n) -> p s n", s=2)
        sqj = work[:, 11264:11264 + CH]

        ssq = small[:, 0:NT]
        rstd = small[:, NT:2 * NT]
        lnh = small[:, 0:16]
        var = small[:, 16:16 + NT]
        ones = par[:].rearrange("p k n -> p (k n)")[:, 0:P]
        mn = small[:, 24:27]
        rsum = small[:, 27:30]
        rinv = small[:, 30:33]
        half = small[:, 33:34]
        ssf = small[:, 24:26]
        rsf = small[:, 27:29]

        pg = [ctx.enter_context(nc.psum_tensor(f"pg{i}", [P, CH], F32)) for i in range(2)]
        pS = [ctx.enter_context(nc.psum_tensor(f"pS{i}", [P, CH], F32)) for i in range(2)]
        pT = [ctx.enter_context(nc.psum_tensor(f"pT{i}", [P, CH], F32)) for i in range(2)]
        pO = [ctx.enter_context(nc.psum_tensor(f"pO{i}", [P, CH], F32)) for i in range(2)]

        pH = [pT[0], pT[1], pO[0], pO[1]]

        v_d = scratch("v_d", [TOK, D])
        tb_d = scratch("tb_d", [PAIRS, P, TOK])
        c_d = scratch("c_d", [KT, P, TOK])
        za_d = scratch("za_d", [KT, P, TOK])
        ga_d = scratch("ga_d", [KT, P, TOK])
        gb_d = scratch("gb_d", [KT, P, TOK])
        m_d = scratch("m_d", [KT, P, TOK])
        rel_d = scratch("rel_d", [HEADS, QB, RROWS, ECOLS])

        x_in = [sem(f"x_in{t}") for t in range(8)]
        par_in, mask_in, tab_in = sem("par_in"), sem("mask_in"), sem("tab_in")
        const_ok, par_ps, par_ok = sem("const_ok"), sem("par_ps"), sem("par_ok")
        table0, rel_out = sem("table0"), sem("rel_out")
        mask_ok, pads_ok = sem("mask_ok"), sem("pads_ok")
        sq_ok, ms_ok, rstd_ok, xn_ok, ht_ps = (sem(n) for n in ("sq_ok", "ms_ok", "rstd_ok", "xn_ok", "ht_ps"))
        x_hi, x_lo = sem("x_hi"), sem("x_lo")
        w_ld = [sem(f"w_ld{i}") for i in range(2)]
        w_hi, w_lo = sem("w_hi"), sem("w_lo")
        w_used = sem("w_used")
        g_done = sem("g_done")
        g_out = [sem(f"g_out{i}") for i in range(2)]
        th_ok, u_ok, tap_ok = sem("th_ok"), sem("u_ok"), sem("tap_ok")
        st_out = [sem(f"st_out{i}") for i in range(3)]
        tb_out, c_out = sem("tb_out"), sem("c_out")
        cur_ok, curg_ok = sem("cur_ok"), sem("curg_ok")
        v_in, e_in = sem("v_in"), sem("e_in")
        bias_ok = sem("bias_ok")
        qk_done, t_ok, p_exp, inv_ok, p_ok = (sem(n) for n in ("qk_done", "t_ok", "p_exp", "inv_ok", "p_ok"))
        tr_done, pt_ok, pv_done, o_out = (sem(n) for n in ("tr_done", "pt_ok", "pv_done", "o_out"))
        tbs_in, c_in = sem("tbs_in"), sem("c_in")
        g_in = [sem(f"g_in{i}") for i in range(2)]
        m_out = [sem(f"m_out{i}") for i in range(2)]
        m_in = [sem(f"m_in{i}") for i in range(2)]
        ya_t = sem("ya_t")
        za_in = [sem(f"za_in{i}") for i in range(3)]
        ones_ok, lnh_ok, csum, sum_ps, mu_ok, dev, sq_a, sq_v = (
            sem(n) for n in ("ones_ok", "lnh_ok", "csum", "sum_ps", "mu_ok", "dev", "sq_a", "sq_v"))
        var_ok, rcol_ok, diag_ok, lnr_ok, nrm, lth, ly, lw, ta_ok = (
            sem(n) for n in ("var_ok", "rcol_ok", "diag_ok", "lnr_ok", "nrm", "lth", "ly", "lw", "ta_ok"))
        fg_in, xr_in = sem("fg_in"), [sem(f"xr_in{i}") for i in range(4)]
        fsq, fms, frs, fmid, y_ok = (sem(n) for n in ("fsq", "fms", "frs", "fmid", "y_ok"))
        y_out = [sem(f"y_out{i}") for i in range(2)]

        def w_tile(w, col):
            return w.rearrange("(k p) c -> p k c", p=P)[:, :, bass.ds(col, P)]

        def w_rows(w, col, s):
            return w.rearrange("(k p) c -> p k c", p=P)[:, 2 * s:2 * s + 2, col:col + CH]

        w0 = w_in[0]

        def tok_rows(prompt, sample, t):
            if t < PROMPT // P:
                return prompt[0, t * P:(t + 1) * P, :]
            return sample[0, t * P - PROMPT:(t + 1) * P - PROMPT, :]

        def row_of(a, i):
            return a[bass.ds(i, 1)].rearrange("a p n -> (a p) n")

        def chunk(n):
            return slice(n * CH, (n + 1) * CH)

        def grp(i, gi):
            if isinstance(i, int):
                return grs((G_UNIT if i == 0 else G_UNIT1 + 24 * (i - 1)) + gi)
            g = G_UNIT1 - 24 + gi
            return g % 2, 24 * i + (g + 1), 12 * i + (g // 2 + 1)

        def s_of(i):
            return S_UNIT if isinstance(i, int) and i == 0 else S_UNIT1 - 8

        def grs(g):
            return g % 2, g + 1, g // 2 + 1

        def seg_of(b):
            return (b % 12) // 4, b % 4

        def keys_of(b):
            return SEG_ROWS[seg_of(b)[0]] * BAND

        def kind_of(b):
            s, j = seg_of(b)
            return 9 * (b // 12) + 3 * s + JKIND[j]

        def after(eng, sm, count):
            if not isinstance(count, int) or count > 0:
                eng.wait_ge(sm, count)

        block = ctx.enter_context(nc.Block())

        @block.sync
        def _(sp):
            def piece(slot, src, split):
                if split is not None:
                    sp.wait_ge(w_lo, split)
                dst = raw[:, slot, :].rearrange("p (k c) -> p k c", k=src.shape[1])
                sp.dma_start(dst, src).then_inc(w_ld[slot], 16)

            def piece_s(s, src):
                piece(s % 2, src, s - 1 if s >= 2 else None)

            def load_x(n):
                for t in range(4):
                    sp.dma_start(xt[:, n % 2, t, :], tok_rows(x_prompt, x_sample, 4 * n + t)).then_inc(x_in[4 * (n % 2) + t], 16)

            load_x(0)
            sp.dma_start(prow[0:TAPS, :], dw_w[0]).then_inc(par_in, 16)
            for r, src in ((I_DWB, dw_b[0:1, :]), (I_LNG, ln_g[0:1, :]), (I_LNB, ln_b[0:1, :]),
                           (I_NG, norm_g[0:1, :]), (I_BGA, b_gate[0:1, 0:D]), (I_BGB, b_gate[0:1, D:2 * D])):
                sp.dma_start(prow[r:r + 1, :], src).then_inc(par_in, 16)
            for s in range(2):
                piece_s(s, w_rows(w0, C_V * P, s))
            load_x(1)
            for s in range(2, 4):
                piece_s(s, w_rows(w0, C_V * P, s))
            sp.wait_ge(ht_ps, KT)
            load_x(2)
            sp.dma_start(msk32, masks).then_inc(mask_in, 16)
            for s in range(4, 8):
                piece_s(s, w_rows(w0, C_V * P + CH, s - 4))

            def load_rel(h, built):
                after(sp, bias_ok, built)
                for r in range(8):
                    src = rel_d[bass.ds(h, 1), :, 7 - r:7 - r + EROWS, :].rearrange("a c r k -> (a c) r k")
                    sp.dma_start(et[QB * r:QB * r + QB, :, :], src).then_inc(e_in, 16)

            def load_v(i, used):
                after(sp, pv_done, used)
                v4 = v_d.rearrange("(g r t) d -> r t g d", g=6, r=4)
                for j in range(4):
                    for r in range(4):
                        src = v4[r, BAND_START[j]:BAND_START[j] + BAND, :, bass.ds(i * P, P)]
                        sp.dma_start(vb[BAND * r:BAND * r + BAND, :, j, :], src).then_inc(v_in, 16)

            sp.wait_ge(x_lo, 3 * KT)
            sp.wait_ge(rel_out, 16 * QB)
            load_rel(0, 0)
            for s, c in ((8, C_A), (9, C_GLU), (10, C_Q), (11, C_K)):
                piece_s(s, w_tile(w0, c * P))
            for n in range(3):
                sp.wait_ge(st_out[n], 128)
            load_v(0, 0)
            for s, c in ((12, C_ZB), (13, C_ZA)):
                piece_s(s, w_tile(w0, c * P))

            def unit(i):
                col = {T_GA: C_GA - 1, T_GB: C_GB - 1, T_A: C_A + 1, T_GLU: C_GLU + 1, T_Q: C_Q + 1, T_K: C_K + 1,
                       T_GA2: C_GA, T_GB2: C_GB}
                tiles, last = tiles_of(i), isinstance(i, int) and i > 0
                ahead = [col[t] for t in tiles[2:]] + ([] if last else [C_ZB + 1, C_ZA + 1])
                for n, c in enumerate(ahead):
                    s = s_of(i) + n + 2
                    piece(s % 2, w_tile(w0, i * P + c * P), 8 * i + (s - 1))
                    if n == 1:
                        load_rel(2 * i + 1, 18 * i + 9)
                    if n == 3 and not last:
                        load_rel(2 * i + 2, 18 * i + 18)
                    if n == 4 and not last:
                        load_v(i + 1, 24 * i + 24)

            unit(0)
            with sp.Fori(1, PAIRS - 1) as i:
                unit(i)
            unit(PAIRS - 1)

            def piece_y(s):
                if s < S_OUT:
                    piece_s(s, w_tile(w_o_b[0] if s < S_YA else w_pw_a[0], (s - S_YB) % KT * P))
                else:
                    piece_s(s, w_rows(w_out[0], CH * ((s - S_OUT) // 4), (s - S_OUT) % 4))

            piece_y(S_YB)
            piece_y(S_YB + 1)
            sp.wait_ge(tb_out, 16 * (PAIRS - 1))
            sp.wait_ge(pv_done, BLK * PAIRS)
            for k in range(7):
                sp.dma_start(tbs[:, k, :], tb_d[k]).then_inc(tbs_in, 16)
            piece_y(S_YB + 2)
            for n in range(3):
                sp.wait_ge(st_out[n], 128 + 48 * PAIRS)
            sp.wait_ge(tap_ok, TAPS * PAIRS)
            for e in range(2 * 24):
                ct, n = (e % 24) // NCH, e % NCH
                if n == 0:
                    piece_y(S_YB + e // NCH + 3)
                if 2 <= e < 26:
                    sp.wait_ge(m_out[e % 2], 16 * (e // 2))
                elif e >= 26:
                    b, _, out = grs(G_YB + e - 2)
                    sp.wait_ge(g_out[b], out)
                sp.dma_start(gst[:, e % 2, :], (gb_d if e < 24 else ga_d)[ct, :, chunk(n)]).then_inc(g_in[e % 2], 16)
                if e == 24:
                    sp.wait_ge(ta_ok, 3 * KT)
                    for b in range(2):
                        sp.wait_ge(m_out[b], 16 * 12)
                if e >= 24:
                    sp.dma_start(mst[:, e % 2, :], m_d[ct, :, chunk(n)]).then_inc(m_in[e % 2], 16)
                if e == 1:
                    sp.wait_ge(c_out, 32 * PAIRS)
                    sp.wait_ge(x_lo, 6 * KT)
                    for k in range(KT):
                        sp.dma_start(cs[:, k, :], c_d[k]).then_inc(c_in, 16)
            piece_y(S_OUT + 3)
            sp.wait_ge(x_lo, 12 * KT)
            sp.dma_start(fg, final_g.rearrange("(a n) -> a n", a=1).to_broadcast([P, D])).then_inc(fg_in, 16)
            for e in range(2 * NT):
                c, t = e // NT, e % NT
                if e >= 4:
                    b, _, out = grs(G_OUT + e - 4)
                    sp.wait_ge(g_out[b], out)
                sp.dma_start(xre[:, e % 4, :], tok_rows(x_prompt, x_sample, t)[:, c * CH:(c + 1) * CH]).then_inc(
                    xr_in[e % 4], 16)
                if e in (4, 5, 6, 7):
                    piece_y(S_OUT + e) if e < 6 else None
                if e == NT - 1:
                    for s in (6, 7):
                        piece_y(S_OUT + s)

        @block.gpsimd
        def _(pool):
            nc.gpsimd.memset(ident[:], 0.0).then_inc(const_ok, 1)
            nc.gpsimd.memset(half, -0.5).then_inc(const_ok, 1)
            pool.wait_ge(const_ok, 2)
            nc.gpsimd.affine_select(out=ident[:], in_=ident[:], compare_op=ALU.not_equal, fill=1.0, base=0,
                                    pattern=[[-1, P]], channel_multiplier=1).then_inc(const_ok, 1)
            for n in range(NCH):
                pool.wait_ge(ms_ok, n + 1)
                nc.gpsimd.tensor_tensor(rstd[:, 4 * n:4 * n + 4], ssq[:, 4 * n:4 * n + 4],
                                        half.to_broadcast([P, 4]), ALU.pow).then_inc(rstd_ok, 1)
            pool.wait_ge(x_lo, 3 * KT)
            nc.gpsimd.memset(table[0:HEADS, :], 0.0).then_inc(table0, 1)
            pool.wait_ge(table0, 1)
            t3 = table[0:HEADS, :].rearrange("h (r c) -> h r c", r=RROWS)
            pool.dma_start(t3[:, 4:4 + 15, 16:16 + 31], rpb[0]).then_inc(tab_in, 16)
            pool.wait_ge(tab_in, 16)
            for c in range(QB):
                pool.dma_start(rel_d[:, c, :, :], t3[:, :, 15 - c:15 - c + ECOLS]).then_inc(rel_out, 16)
            pool.wait_ge(mask_ok, 1)

            def unit(i):
                for h in range(2):
                    pool.wait_ge(e_in, 256 * i + 128 * (h + 1))
                    for kd in range(KINDS):
                        s, jk = kd // 3, kd % 3
                        nk = SEG_ROWS[s] * BAND
                        used = 12 * h if kd < 3 else 12 * h + 4 * ((kd - 3) // 3) + [0, 2, 3][kd % 3] + 1
                        after(pool, t_ok, 24 * i + used)
                        e = et[:, SEG_E0[s]:SEG_E0[s] + SEG_ROWS[s], 16 - 8 * jk:16 - 8 * jk + BAND]
                        nc.gpsimd.tensor_tensor(
                            bt[:, kd % 3, 0:nk].rearrange("p (r c) -> p r c", c=BAND),
                            mask[:, KIND_OFF[kd]:KIND_OFF[kd] + nk].rearrange("p (r c) -> p r c", c=BAND),
                            e, ALU.subtract).then_inc(bias_ok, 1)

            unit(0)
            with pool.Fori(1, PAIRS) as i:
                unit(i)

            pool.wait_ge(var_ok, 1)
            nc.gpsimd.tensor_tensor(var, var, half.to_broadcast([P, NT]), ALU.pow).then_inc(rcol_ok, 1)
            def load_za(e):
                n, k = e // KT, e % KT
                pool.dma_start(tmp3[:, chunk(e % 3)], za_d[k, :, chunk(n)]).then_inc(za_in[e % 3], 16)

            pool.wait_ge(sum_ps, 2 * NCH + 1)
            for n in range(3):
                pool.wait_ge(st_out[n], 128 + 48 * PAIRS)
            for e in range(3):
                load_za(e)
            for e in range(3 * KT):
                n, k = e // KT, e % KT
                pool.wait_ge(lw, e + 1)
                pool.wait_ge(za_in[e % 3], 16 * (e // 3 + 1))
                nc.gpsimd.tensor_tensor(cs[:, k, chunk(n)], cs[:, k, chunk(n)], tmp3[:, chunk(e % 3)],
                                        ALU.mult).then_inc(ta_ok, 1)
                if e + 3 < 3 * KT:
                    pool.wait_ge(ta_ok, e + 1)
                    load_za(e + 3)
            for t in range(NT):
                pool.wait_ge(fms, t + 1)
                nc.gpsimd.tensor_tensor(rsf[:, t % 2:t % 2 + 1], ssf[:, t % 2:t % 2 + 1], half,
                                        ALU.pow).then_inc(frs, 1)

        @block.scalar
        def _(act):
            def split_hi(s, loaded, free_sem, free):
                act.wait_ge(w_ld[s % 2], loaded)
                if free_sem is not None:
                    act.wait_ge(free_sem, free)
                nc.scalar.activation(ws[:, s % 4, 0, :], raw[:, s % 2, :], ACT.Copy).then_inc(w_hi, 1)

            def split_s(s, free_sem=None, free=0):
                if s >= S_PRO + 4 and s < S_OUT + 4:
                    free_sem, free = g_done, piece_done(s - 4)
                split_hi(s, 16 * (s // 2 + 1), free_sem, free)

            def squares(n):
                for t in range(4):
                    act.wait_ge(x_in[4 * (n % 2) + t], 16 * (n // 2 + 1))
                    if 4 * n + t:
                        act.wait_ge(sq_ok, 4 * n + t)
                    nc.scalar.activation(junk, xt[:, n % 2, t, :], ACT.Square,
                                         accum_out=ssq[:, 4 * n + t:4 * n + t + 1]).then_inc(sq_ok, 1)

            def h_hi(n, k):
                act.wait_ge(ht_ps, KT * n + k + 1)
                nc.scalar.activation(xs[:, k, 0, chunk(n)], pH[k % 4][:], ACT.Copy,
                                     scale=par[:, k, I_NG:I_NG + 1]).then_inc(x_hi, 1)

            def take_v(g):
                b, done, out = grs(g)
                act.wait_ge(g_done, done)
                if g >= 3:
                    act.wait_ge(st_out[g % 3], 16 * (g // 3))
                nc.scalar.activation(stage[:, g % 3, :], pg[b][:], ACT.Copy, scale=0.5).then_inc(g_out[b], 1)
                act.wait_ge(g_out[b], out)
                t, c = g % NT, g // NT
                act.dma_start(v_d[t * P:(t + 1) * P, chunk(c)], stage[:, g % 3, :]).then_inc(st_out[g % 3], 16)

            squares(0)
            split_s(0)
            split_s(1)
            act.wait_ge(par_ok, 1)
            for k in range(KT):
                h_hi(0, k)
            split_s(2)
            split_s(3)
            for n in range(NCH):
                if n + 1 < NCH:
                    squares(n + 1)
                for j in range(4):
                    if 4 * n + j < NT - 1:
                        take_v(4 * n + j)
                    if n + 1 < NCH:
                        for k in h_tiles(j):
                            h_hi(n + 1, k)
            for j in range(3):
                split_s(4 + j, w_used, j + 1)
            take_v(NT - 1)
            split_s(7, g_done, NT)
            for t in range(NT - 1):
                take_v(NT + t)
            for j in range(3):
                split_s(8 + j, w_used, 4 + j)
            take_v(2 * NT - 1)
            split_s(11, g_done, 2 * NT)

            def take_a(b, done, n):
                act.wait_ge(g_done, done)
                off = PAD + n * CH + (PAD if n else 0)
                nc.scalar.activation(u[:, off:off + CH], pg[b][:], ACT.Copy, scale=0.5).then_inc(g_out[b], 1)

            def take_q(b, done, n, before=None):
                act.wait_ge(g_done, done)
                if before is not None:
                    act.wait_ge(qk_done, before)
                nc.scalar.activation(qT[:, chunk(n)].rearrange("p (j r c) -> p j r c", j=4, c=QB),
                                     pg[b][:].rearrange("p (r j c) -> p j r c", j=4, c=QB), ACT.Copy,
                                     scale=-(HD ** -0.5)).then_inc(g_out[b], 1)

            def take_k(b, done, n):
                act.wait_ge(g_done, done)
                nc.scalar.activation(kT[:, chunk(n)], pg[b][:], ACT.Copy).then_inc(g_out[b], 1)

            act.wait_ge(pads_ok, 3)
            act.wait_ge(rel_out, 16 * QB)
            for n in range(NCH):
                take_a(*grs(G_PRO + n)[:2], n)
            split_s(12)
            for n in range(NCH):
                b, done, _ = grs(G_PRO + NCH + n)
                act.wait_ge(g_done, done)
                act.wait_ge(st_out[n], 128)
                nc.scalar.activation(stage[:, n, :], pg[b][:], ACT.Tanh, scale=0.5).then_inc(g_out[b], 1)
            split_s(13)
            for n in range(NCH):
                take_q(*grs(G_PRO + 2 * NCH + n)[:2], n)
            for n in range(NCH):
                take_k(*grs(G_PRO + 3 * NCH + n)[:2], n)

            def refill_hi(phase, n, src_of, scale):
                g_next = {1: G_YB, 2: G_YA, 3: G_OUT}[phase]
                act.wait_ge(g_done, g_next - NCH + n + 1)
                for k in range(KT):
                    if phase == 2:
                        act.wait_ge(ta_ok, KT * n + k + 1)
                    if phase == 3 and k == KT - 1:
                        b, _, out = grs(G_OUT - NCH + n)
                        act.wait_ge(g_out[b], out)
                    nc.scalar.activation(xs[:, k, 0, chunk(n)], src_of(k), ACT.Copy, scale=scale).then_inc(x_hi, 1)

            def refill_tb(n):
                if n == 0:
                    act.wait_ge(tbs_in, 16 * 7)
                    act.wait_ge(o_out, 6 * PAIRS)
                refill_hi(1, n, lambda k: tbs[:, k, chunk(n)] if k < 7 else tb[:, chunk(n)], 1.0)

            def unit(i):
                tiles = tiles_of(i)
                first, last = tiles is FIRST_UNIT, tiles is LAST_UNIT
                stored = 128 if first else 128 + 16 - 48

                def gate_bias(ct):
                    nc.scalar.activation(cur[:, TAPS + 1:TAPS + 3],
                                         par[:, bass.ds(ct, 1), I_BGA:I_BGA + 2].rearrange("p a n -> p (a n)"),
                                         ACT.Copy, scale=0.5).then_inc(curg_ok, 1)

                if not first:
                    gate_bias(i - 1)

                def evac(gi):
                    tile, n = tiles[gi // NCH], gi % NCH
                    b, done, out = grp(i, gi)
                    st = stage[:, n, :]
                    if tile == T_Q:
                        take_q(b, done, n, 24 * i + 24)
                        return
                    if tile == T_K:
                        take_k(b, done, n)
                        return
                    if tile == T_A:
                        act.wait_ge(tap_ok, TAPS * i + TAPS)
                        take_a(b, done, n)
                        return
                    act.wait_ge(g_done, done)
                    if tile == T_ZB:
                        act.wait_ge(u_ok, 3 * i + (n + 1))
                        nc.scalar.activation(st, pg[b][:], ACT.Tanh, scale=0.5).then_inc(th_ok, 1)
                    elif tile == T_ZA:
                        bz, _, oz = grp(i, n)
                        act.wait_ge(g_out[bz], oz)
                        nc.scalar.activation(st, pg[b][:], ACT.Tanh, scale=0.5).then_inc(th_ok, 1)
                    elif tile == T_GLU:
                        act.wait_ge(st_out[n], 48 * i + (stored + (16 if first else 48)))
                        nc.scalar.activation(st, pg[b][:], ACT.Tanh, scale=0.5).then_inc(g_out[b], 1)
                    else:
                        order = {T_GA: 1, T_GB: 2, T_GA2: 3, T_GB2: 4}[tile]
                        act.wait_ge(st_out[n], 48 * i + (stored + 16 * order))
                        if gi == 2 * NCH:
                            act.wait_ge(curg_ok, i)
                        if gi == 4 * NCH:
                            gate_bias(i)
                            act.wait_ge(curg_ok, i + 1)
                        g = TAPS + 1 + (order - 1) % 2
                        nc.scalar.activation(st, pg[b][:], ACT.Tanh, scale=0.5,
                                             bias=cur[:, g:g + 1]).then_inc(g_out[b], 1)

                def store(gi):
                    tile, n = tiles[gi // NCH], gi % NCH
                    dst, ct = {T_ZA: (za_d, i), T_GA: (ga_d, i - 1), T_GB: (gb_d, i - 1), T_GA2: (ga_d, i),
                               T_GB2: (gb_d, i)}[tile]
                    b, _, out = grp(i, gi)
                    act.wait_ge(g_out[b], out)
                    act.dma_start(row_of(dst, ct)[:, chunk(n)], stage[:, n, :]).then_inc(st_out[n], 16)

                def probs(b):
                    act.wait_ge(t_ok, 24 * i + (b + 1))
                    t = tt[:, b % 3, 0:keys_of(b)]
                    nc.scalar.activation(t, t, ACT.Exp, scale=-1.0, bias=mn[:, b % 3:b % 3 + 1],
                                         accum_out=rsum[:, b % 3:b % 3 + 1]).then_inc(p_exp, 1)

                def probs_t(b):
                    act.wait_ge(tr_done, 24 * i + (b + 1))
                    after(act, pv_done, 24 * i + max(b - 1, 0))
                    nk = keys_of(b)
                    nc.scalar.activation(pt[:, b % 2, 0:nk], pT[b % 2][:, 0:nk], ACT.Copy).then_inc(pt_ok, 1)

                for slot in range(2 * NCH * len(tiles)):
                    gi, hf = slot // 2, slot % 2
                    pos, n = gi // NCH, gi % NCH
                    if hf == 0 and gi >= 1:
                        evac(gi - 1)
                    if slot < BLK:
                        probs(slot)
                    if 1 <= slot <= BLK:
                        probs_t(slot - 1)
                    if hf == 1 and gi >= 1 and tiles[(gi - 1) // NCH] in (T_ZA, T_GA, T_GB, T_GA2, T_GB2):
                        store(gi - 1)
                    if n == 1 and hf == 0:
                        s = s_of(i) + pos + 2
                        split_hi(s, 64 * i + 16 * (s // 2 + 1), g_done, 24 * i + piece_done(s - 4))
                    if slot == BLK + 1:
                        act.wait_ge(tap_ok, TAPS * i + TAPS)
                        act.dma_start(row_of(c_d, i)[:, 0:PROMPT], cv[:, 0:PROMPT]).then_inc(c_out, 16)
                        act.dma_start(row_of(c_d, i)[:, PROMPT:TOK], cv[:, PROMPT + PAD:CLEN]).then_inc(c_out, 16)
                    if slot == BLK + 3 and not last:
                        act.wait_ge(o_out, 6 * i + 6)
                        act.dma_start(row_of(tb_d, i), tb).then_inc(tb_out, 16)
                    if last and pos == 5 and hf == 1 and n >= 1:
                        refill_tb(n - 1)
                evac(NCH * len(tiles) - 1)
                if last:
                    store(NCH * len(tiles) - 1)
                    refill_tb(2)

            unit(0)
            with act.Fori(1, PAIRS - 1) as i:
                unit(i)
            unit(PAIRS - 1)

            def layernorm(step):
                if step == 9:
                    for n in range(NCH):
                        act.wait_ge(sum_ps, n + 1)
                        nc.scalar.activation(lnB[:, chunk(n)], pS[n % 2][:], ACT.Copy, scale=1.0 / D).then_inc(mu_ok, 1)
                if 10 <= step < 14:
                    for k in range(2 * (step - 10), 2 * (step - 10) + 2):
                        act.wait_ge(dev, k + 1)
                        if k >= 2:
                            act.wait_ge(sq_v, k - 1)
                        nc.scalar.activation(tmp3 if k else lnA, cs[:, k, :], ACT.Square).then_inc(sq_a, 1)
                if step == 14:
                    act.wait_ge(sum_ps, NCH + 1)
                    nc.scalar.activation(var, pS[1][:, 0:NT], ACT.Copy, scale=1.0 / D, bias=LN_EPS).then_inc(var_ok, 1)
                if step == 15:
                    for n in range(NCH):
                        act.wait_ge(sum_ps, NCH + n + 2)
                        nc.scalar.activation(lnB[:, chunk(n)], pS[n % 2][:], ACT.Copy).then_inc(lnr_ok, 1)
                if 16 <= step < 24:
                    for e in range(3 * (step - 16), 3 * (step - 16) + 3):
                        n, k = e // KT, e % KT
                        c = cs[:, k, chunk(n)]
                        act.wait_ge(nrm, e + 1)
                        if e == 0:
                            act.wait_ge(lnh_ok, 1)
                        if e >= 3:
                            act.wait_ge(lw, e - 2)
                        g2, b2 = lnh[:, k:k + 1], lnh[:, 8 + k:9 + k]
                        nc.scalar.activation(lnA[:, chunk(e % 3)], c, ACT.Tanh, scale=g2, bias=b2).then_inc(lth, 1)
                        act.wait_ge(lth, e + 1)
                        nc.scalar.activation(c, c, ACT.Identity, scale=g2, bias=b2).then_inc(ly, 1)

            def store_m(gi):
                b, _, out = grs(G_YB + gi)
                act.wait_ge(g_out[b], out)
                act.dma_start(m_d[gi // NCH, :, chunk(gi % NCH)], gst[:, gi % 2, :]).then_inc(m_out[gi % 2], 16)

            for g0, s0 in ((G_YB, S_YB), (G_YA, S_YA)):
                phase = 2 if g0 == G_YB else 3
                for gi in range(24):
                    tile, n = gi // NCH, gi % NCH
                    if n == 1:
                        split_s(s0 + tile + 2)
                    if phase == 2:
                        if gi >= 1:
                            store_m(gi - 1)
                        layernorm(gi)
                    if tile == KT - 1 and n >= 1:
                        refill_hi(phase, n - 1, lambda k: cs[:, k, chunk(n - 1)], 0.5)
                        if n == 2 and phase == 3:
                            split_s(S_OUT + 2)
                if phase == 2:
                    store_m(23)
                else:
                    split_s(S_OUT + 3)
                refill_hi(phase, 2, lambda k: cs[:, k, chunk(2)], 0.5)

            for e in range(2 * NT):
                c, t = e // NT, e % NT
                b, _, out = grs(G_OUT + e)
                act.wait_ge(g_out[b], out)
                src = res[:, t, :] if c == 0 else yst[:, t % 2, CH:D]
                acc = ssq[:, t:t + 1] if c == 0 else rstd[:, t:t + 1]
                if e:
                    act.wait_ge(fsq, e)
                nc.scalar.activation(sqj, src, ACT.Square, accum_out=acc).then_inc(fsq, 1)
                if e == NT - 2:
                    for j in range(3):
                        split_s(S_OUT + 4 + j, w_used, 7 + j)
                if e == NT - 1:
                    split_s(S_OUT + 7, g_done, G_OUT + NT)
                if c == 1 and t >= 1:
                    act.wait_ge(y_ok, 2 * t)
                    act.dma_start(tok_rows(y_prompt, y_sample, t - 1), yst[:, (t - 1) % 2, :]).then_inc(
                        y_out[(t - 1) % 2], 16)
            act.wait_ge(y_ok, 2 * NT)
            act.dma_start(tok_rows(y_prompt, y_sample, NT - 1), yst[:, (NT - 1) % 2, :]).then_inc(
                y_out[(NT - 1) % 2], 16)
            for b in range(2):
                act.wait_ge(y_out[b], 16 * NT // 2)

        @block.vector
        def _(dve):
            def split_lo(s, hi):
                dve.wait_ge(w_hi, hi)
                nc.vector.tensor_tensor(ws[:, s % 4, 1, :], raw[:, s % 2, :], ws[:, s % 4, 0, :].bitcast(F32),
                                        ALU.subtract).then_inc(w_lo, 1)

            def split_s(s):
                split_lo(s, s + 1)

            def refill_lo(phase, n, src_of, scale):
                for k in range(KT):
                    dve.wait_ge(x_hi, 24 * phase + KT * n + k + 1)
                    nc.vector.scalar_tensor_tensor(xs[:, k, 1, chunk(n)], src_of(k), scale,
                                                   xs[:, k, 0, chunk(n)].bitcast(F32), ALU.mult,
                                                   ALU.subtract).then_inc(x_lo, 1)

            def normalise(n):
                dve.wait_ge(sq_ok, 4 * n + 4)
                s4 = ssq[:, 4 * n:4 * n + 4]
                nc.vector.tensor_scalar(s4, s4, 1.0 / D, RMS_EPS, ALU.mult, ALU.add).then_inc(ms_ok, 1)
                dve.wait_ge(rstd_ok, n + 1)
                for t in range(4):
                    x = xt[:, n % 2, t, :]
                    nc.vector.tensor_scalar(x, x, rstd[:, 4 * n + t:4 * n + t + 1], None, ALU.mult).then_inc(xn_ok, 1)

            def h_lo(n, k):
                dve.wait_ge(x_hi, KT * n + k + 1)
                nc.vector.scalar_tensor_tensor(xs[:, k, 1, chunk(n)], pH[k % 4][:], par[:, k, I_NG:I_NG + 1],
                                               xs[:, k, 0, chunk(n)].bitcast(F32), ALU.mult,
                                               ALU.subtract).then_inc(x_lo, 1)

            dve.wait_ge(par_ps, 1)
            nc.vector.tensor_copy(par[:].rearrange("p k n -> p (k n)"), pT[0][:, 0:KT * NPAR]).then_inc(par_ok, 1)
            normalise(0)
            split_s(0)
            split_s(1)
            dve.wait_ge(par_ok, 1)
            for k in range(KT):
                h_lo(0, k)
            split_s(2)
            split_s(3)
            for n in range(1, NCH):
                normalise(n)
                for k in range(KT):
                    h_lo(n, k)
            dve.wait_ge(mask_in, 16)
            nc.vector.tensor_copy(mask, msk32).then_inc(mask_ok, 1)
            dve.wait_ge(mask_ok, 1)
            nc.vector.memset(u[:, 0:PAD], 0.0).then_inc(pads_ok, 1)
            nc.vector.memset(u[:, PAD + PROMPT:2 * PAD + PROMPT], 0.0).then_inc(pads_ok, 1)
            nc.vector.memset(u[:, ULEN - PAD:ULEN], 0.0).then_inc(pads_ok, 1)
            for s in range(4, 12):
                split_s(s)

            def load_taps(ct, before):
                after(dve, tap_ok, before)
                nc.vector.tensor_copy(cur[:, 0:TAPS + 1], par[:, bass.ds(ct, 1), 0:TAPS + 1].rearrange(
                    "p a n -> p (a n)")).then_inc(cur_ok, 1)

            def tap(i, k):
                if k == 0:
                    dve.wait_ge(u_ok, 3 * i + 3)
                    dve.wait_ge(cur_ok, i + 1)
                    after(dve, c_out, 32 * i)
                    nc.vector.tensor_scalar(cv[:, 0:CLEN], u[:, 0:CLEN], cur[:, 0:1], cur[:, TAPS:TAPS + 1],
                                            ALU.mult, ALU.add).then_inc(tap_ok, 1)
                else:
                    dve.wait_ge(tap_ok, TAPS * i + k)
                    nc.vector.scalar_tensor_tensor(cv[:, 0:CLEN], u[:, k:k + CLEN], cur[:, k:k + 1],
                                                   cv[:, 0:CLEN], ALU.mult, ALU.add).then_inc(tap_ok, 1)

            def glu(ga, out, n):
                dve.wait_ge(g_out[ga[0]], ga[2])
                dve.wait_ge(g_out[out[0]], out[2])
                off = PAD + n * CH + (PAD if n else 0)
                nc.vector.scalar_tensor_tensor(u[:, off:off + CH], stage[:, n, :], 1.0, u[:, off:off + CH], ALU.add,
                                               ALU.mult).then_inc(u_ok, 1)

            load_taps(0, 0)
            split_s(12)
            for n in range(NCH):
                glu(grs(G_PRO + n), grs(G_PRO + NCH + n), n)
            split_s(13)
            for k in range(EARLY0):
                tap(0, k)

            def unit(i):
                tiles = tiles_of(i)
                last = tiles is LAST_UNIT
                slots = 2 * NCH * len(tiles)

                def scores(b):
                    nk = keys_of(b)
                    dve.wait_ge(qk_done, 24 * i + (b + 1))
                    dve.wait_ge(bias_ok, 18 * i + (kind_of(b) + 1))
                    after(dve, tr_done, 24 * i + max(b - 2, 0))
                    dve.nop(nofuse=True)
                    nc.vector.tensor_tensor_reduce(
                        out=tt[:, b % 3, 0:nk], in0=pS[b % 2][:, 0:nk], in1=bt[:, kind_of(b) % 3, 0:nk], scale=1.0,
                        scalar=3e38, op0=ALU.add, op1=ALU.min, accum_out=mn[:, b % 3:b % 3 + 1]).then_inc(t_ok, 1)

                def probs(b):
                    t = tt[:, b % 3, 0:keys_of(b)]
                    dve.wait_ge(p_exp, 24 * i + (b + 1))
                    nc.vector.reciprocal(rinv[:, b % 3:b % 3 + 1], rsum[:, b % 3:b % 3 + 1]).then_inc(inv_ok, 1)
                    dve.wait_ge(inv_ok, 24 * i + (b + 1))
                    nc.vector.tensor_scalar(t, t, rinv[:, b % 3:b % 3 + 1], None, ALU.mult).then_inc(p_ok, 1)

                def take_o(q):
                    h, s = q // 3, q % 3
                    rows = slice(HD * h, HD * h + HD)
                    dve.wait_ge(pv_done, 24 * i + (4 * q + 4))
                    bz, _, oz = grp(i, s)
                    dve.wait_ge(g_out[bz], oz)
                    z = tb[rows, chunk(s)].rearrange("p (r j c) -> p j r c", j=4, c=QB)
                    o = pO[q % 2][rows, :].rearrange("p (j r c) -> p j r c", j=4, c=QB)
                    nc.vector.tensor_tensor(z, o, z, ALU.mult).then_inc(o_out, 1)

                def evac(gi):
                    tile, n = tiles[gi // NCH], gi % NCH
                    b = grp(i, gi)[0]
                    st = stage[:, n, :]
                    if tile == T_ZB:
                        dve.wait_ge(th_ok, 6 * i + (n + 1))
                        after(dve, tb_out, 16 * i)
                        nc.vector.scalar_tensor_tensor(tb[:, chunk(n)], st, 1.0, pg[b][:], ALU.add,
                                                       ALU.mult).then_inc(g_out[b], 1)
                    elif tile == T_ZA:
                        dve.wait_ge(th_ok, 6 * i + (NCH + n + 1))
                        nc.vector.scalar_tensor_tensor(st, st, 1.0, pg[b][:], ALU.add, ALU.mult).then_inc(g_out[b], 1)
                    elif tile == T_GLU:
                        glu(grp(i, gi - NCH), grp(i, gi), n)

                for slot in range(slots):
                    gi, hf = slot // 2, slot % 2
                    pos, n = gi // NCH, gi % NCH
                    if slot < BLK:
                        scores(slot)
                    if hf == 0 and gi >= 1:
                        evac(gi - 1)
                    if slot < BLK:
                        probs(slot)
                    if n == 1 and hf == 0:
                        s = s_of(i) + pos + 2
                        split_lo(s, 8 * i + (s + 1))
                    if 6 <= slot <= BLK + 2 and slot % 4 == 2:
                        take_o((slot - 6) // 4)
                    if slot < BLK:
                        for k in late_taps(i, slot):
                            tap(i, k)
                    if not last and slot == BLK + 1:
                        load_taps(i + 1, TAPS * i + TAPS)
                    if not last and slot >= slots - EARLY:
                        tap(i + 1, slot - (slots - EARLY))
                    if last and pos == 5 and hf == 1 and n >= 1:
                        refill_tb(n - 1)
                evac(NCH * len(tiles) - 1)
                if last:
                    refill_tb(2)

            def refill_tb(n):
                refill_lo(1, n, lambda k: tbs[:, k, chunk(n)] if k < 7 else tb[:, chunk(n)], 1.0)

            unit(0)
            with dve.Fori(1, PAIRS - 1) as i:
                unit(i)
            unit(PAIRS - 1)

            nc.vector.tensor_scalar(lnh.rearrange("p (n k) -> p k n", n=2), par[:, :, I_LNG:I_LNB + 1], 0.5, None,
                                    ALU.mult).then_inc(lnh_ok, 1)
            dve.wait_ge(lnh_ok, 1)
            dve.wait_ge(curg_ok, PAIRS)
            nc.vector.memset(ones, 1.0).then_inc(ones_ok, 1)

            def layernorm(step):
                if 4 <= step < 8:
                    for k in range(2 * (step - 4) + 1, min(2 * (step - 4) + 3, KT)):
                        if k == 1:
                            dve.wait_ge(c_in, 16 * KT)
                        else:
                            dve.wait_ge(csum, k - 1)
                        nc.vector.tensor_tensor(lnA, cs[:, 0, :] if k == 1 else lnA, cs[:, k, :],
                                                ALU.add).then_inc(csum, 1)
                if 10 <= step < 14:
                    for k in range(2 * (step - 10), 2 * (step - 10) + 2):
                        if k == 0:
                            dve.wait_ge(mu_ok, 3)
                        nc.vector.tensor_tensor(cs[:, k, :], cs[:, k, :], lnB, ALU.subtract).then_inc(dev, 1)
                        if k >= 2:
                            add_square(k - 1)
                if step == 14:
                    add_square(KT - 1)
                if step == 15:
                    dve.wait_ge(rcol_ok, 1)
                    nc.vector.tensor_tensor(diag, ident[:].unsqueeze(1).to_broadcast([P, NT, P]),
                                            var.unsqueeze(2).to_broadcast([P, NT, P]), ALU.mult).then_inc(diag_ok, 1)
                if 16 <= step < 24:
                    for e in range(3 * (step - 16), 3 * (step - 16) + 3):
                        n, k = e // KT, e % KT
                        c = cs[:, k, chunk(n)]
                        if e % KT == 0:
                            dve.wait_ge(lnr_ok, n + 1)
                        nc.vector.tensor_tensor(c, c, lnB[:, chunk(n)], ALU.mult).then_inc(nrm, 1)
                        if e >= 1:
                            swish(e - 1)
                if step == 24:
                    swish(3 * KT - 1)

            def add_square(k):
                dve.wait_ge(sq_a, k + 1)
                if k >= 2:
                    dve.wait_ge(sq_v, k - 1)
                nc.vector.tensor_tensor(lnA, lnA, tmp3, ALU.add).then_inc(sq_v, 1)

            def swish(e):
                n, k = e // KT, e % KT
                dve.wait_ge(ly, e + 1)
                c = cs[:, k, chunk(n)]
                nc.vector.scalar_tensor_tensor(c, lnA[:, chunk(e % 3)], 1.0, c, ALU.add, ALU.mult).then_inc(lw, 1)

            def gate(e):
                b, done, _ = grs(G_YB + e)
                dve.wait_ge(g_done, done)
                dve.wait_ge(g_in[e % 2], 16 * (e // 2 + 1))
                g = gst[:, e % 2, :]
                if e < 24:
                    nc.vector.scalar_tensor_tensor(g, g, 1.0, pg[b][:], ALU.add, ALU.mult).then_inc(g_out[b], 1)
                    return
                nc.vector.scalar_tensor_tensor(g, g, 1.0, pg[b][:], ALU.add, ALU.mult).then_inc(ya_t, 1)
                dve.wait_ge(ya_t, e - 23)
                dve.wait_ge(m_in[e % 2], 16 * (e // 2 - 11))
                ct, n = (e - 24) // NCH, e % NCH
                nc.vector.tensor_tensor(cs[:, ct, chunk(n)], g, mst[:, e % 2, :], ALU.add).then_inc(g_out[b], 1)

            for phase, e0, s0 in ((2, 0, S_YB), (3, 24, S_YA)):
                for gi in range(24):
                    tile, n = gi // NCH, gi % NCH
                    if gi >= 1:
                        gate(e0 + gi - 1)
                    if n == 1:
                        split_s(s0 + tile + 2)
                    if phase == 2:
                        layernorm(gi)
                    if tile == KT - 1 and n >= 1:
                        refill_lo(phase, n - 1, lambda k: cs[:, k, chunk(n - 1)], 0.5)
                        if n == 2 and phase == 3:
                            split_s(S_OUT + 2)
                if phase == 2:
                    layernorm(24)
                gate(e0 + 23)
                if phase == 3:
                    split_s(S_OUT + 3)
                refill_lo(phase, 2, lambda k: cs[:, k, chunk(2)], 0.5)

            def finish(t):
                dve.wait_ge(frs, t + 1)
                r = rsf[:, t % 2:t % 2 + 1]
                nc.vector.scalar_tensor_tensor(yst[:, t % 2, 0:CH], res[:, t, :], r, fg[:, 0:CH], ALU.mult,
                                               ALU.mult).then_inc(y_ok, 1)
                nc.vector.scalar_tensor_tensor(yst[:, t % 2, CH:D], yst[:, t % 2, CH:D], r, fg[:, CH:D], ALU.mult,
                                               ALU.mult).then_inc(y_ok, 1)

            def mean_square(t):
                dve.wait_ge(fsq, NT + t + 1)
                s = ssf[:, t % 2:t % 2 + 1]
                nc.vector.tensor_tensor(s, ssq[:, t:t + 1], rstd[:, t:t + 1], ALU.add).then_inc(fmid, 1)
                dve.wait_ge(fmid, t + 1)
                nc.vector.tensor_scalar(s, s, 1.0 / D, RMS_EPS, ALU.mult, ALU.add).then_inc(fms, 1)

            for e in range(2 * NT):
                c, t = e // NT, e % NT
                b, done, _ = grs(G_OUT + e)
                dve.wait_ge(g_done, done)
                dve.wait_ge(xr_in[e % 4], 16 * (e // 4 + 1))
                if e == NT:
                    dve.wait_ge(fg_in, 16)
                if c == 1 and t >= 2:
                    dve.wait_ge(y_out[t % 2], 16 * (t // 2))
                dst = res[:, t, :] if c == 0 else yst[:, t % 2, CH:D]
                nc.vector.tensor_tensor(dst, pg[b][:], xre[:, e % 4, :], ALU.add).then_inc(g_out[b], 1)
                if e == NT - 2:
                    for j in range(3):
                        split_s(S_OUT + 4 + j)
                if e == NT - 1:
                    split_s(S_OUT + 7)
                if c == 1:
                    mean_square(t)
                    if t >= 1:
                        finish(t - 1)
            finish(NT - 1)

        @block.tensor
        def _(pe):
            PASSES = ((1, 0), (0, 1), (0, 0))

            def half_group(b, s, n, hf, ready=None):
                for k in range(4 * hf, 4 * hf + 4):
                    if ready is not None:
                        pe.wait_ge(x_lo, ready + k + 1)
                    for wpart, xpart in PASSES:
                        last = nc.tensor.matmul(pg[b][:], ws[:, s % 4, wpart, k * P:(k + 1) * P],
                                                xs[:, k, xpart, chunk(n)], start=(k == 0 and wpart == 1),
                                                stop=(k == KT - 1 and (wpart, xpart) == (0, 0)))
                return last

            def token_group(g, s0, t, phase, first):
                b = g % 2
                if g >= 2:
                    pe.wait_ge(g_out[b], g // 2)
                for k in range(KT):
                    if t == 0 and k % 2 == 0:
                        pe.wait_ge(w_lo, s0 + k // 2 + 1)
                    if first:
                        pe.wait_ge(x_lo, 24 * phase + KT * (t // 4) + k + 1)
                    for xpart, wpart in PASSES:
                        last = nc.tensor.matmul(pg[b][:], xs[:, k, xpart, t * P:(t + 1) * P],
                                                ws[:, k // 2, wpart, chunk(k % 2)], start=(k == 0 and xpart == 1),
                                                stop=(k == KT - 1 and (xpart, wpart) == (0, 0)))
                    if t == NT - 1 and k in (1, 3, 5):
                        last.then_inc(w_used, 1)
                last.then_inc(g_done, 1)

            pe.wait_ge(par_in, 16 * 7)
            pe.wait_ge(const_ok, 3)
            for k in range(KT):
                last = nc.tensor.transpose(pT[0][:, k * NPAR:(k + 1) * NPAR], prow[0:NPAR, k * P:(k + 1) * P],
                                           ident[0:NPAR, 0:NPAR])
            last.then_inc(par_ps, 1)
            pe.wait_ge(par_ok, 1)

            def h_t(n, k):
                pe.wait_ge(xn_ok, 4 * n + 4)
                if KT * n + k >= 4:
                    pe.wait_ge(x_lo, KT * n + k - 3)
                for t in range(4):
                    last = nc.tensor.transpose(pH[k % 4][:, t * P:(t + 1) * P], xt[:, n % 2, t, k * P:(k + 1) * P],
                                               ident[:])
                last.then_inc(ht_ps, 1)

            for k in range(KT):
                h_t(0, k)
            for n in range(NCH):
                for j in range(4):
                    token_group(4 * n + j, 0, 4 * n + j, 0, True)
                    if n + 1 < NCH:
                        for k in h_tiles(j):
                            h_t(n + 1, k)
            for t in range(NT):
                token_group(NT + t, 4, t, 0, False)
            for m in range(4):
                for n in range(NCH):
                    g = G_PRO + NCH * m + n
                    if n == 0:
                        pe.wait_ge(w_lo, S_PRO + m + 1)
                    pe.wait_ge(g_out[g % 2], g // 2)
                    half_group(g % 2, S_PRO + m, n, 0)
                    half_group(g % 2, S_PRO + m, n, 1).then_inc(g_done, 1)

            def unit(i):
                tiles = tiles_of(i)

                def scores(b):
                    h, (s, j) = b // 12, seg_of(b)
                    nk, rows = keys_of(b), slice(HD * h, HD * h + HD)
                    if b == 0:
                        for gi in (-2, -1):
                            bank, _, out = grp(i, gi)
                            pe.wait_ge(g_out[bank], out)
                    after(pe, t_ok, 24 * i + max(b - 1, 0))
                    q = qT[rows, s * CH + j * P:s * CH + (j + 1) * P]
                    k = kT[rows, SEG_KEY0[s]:SEG_KEY0[s] + SEG_ROWS[s] * GRID].rearrange("p (r c) -> p r c", c=GRID)
                    k = k[:, :, BAND_START[j]:BAND_START[j] + BAND]
                    nc.tensor.matmul(pS[b % 2][:, 0:nk], q, k, start=True, stop=True).then_inc(qk_done, 1)

                def transposes(b):
                    pe.wait_ge(p_ok, 24 * i + (b + 1))
                    after(pe, pt_ok, 24 * i + max(b - 1, 0))
                    for c in range(keys_of(b) // P):
                        mm = nc.tensor.transpose(pT[b % 2][:, c * P:(c + 1) * P], tt[:, b % 3, c * P:(c + 1) * P],
                                                 ident[:])
                    mm.then_inc(tr_done, 1)

                def values(b):
                    h, (s, j), q = b // 12, seg_of(b), b // 4
                    rows, nc_ = slice(HD * h, HD * h + HD), keys_of(b) // P
                    pe.wait_ge(pt_ok, 24 * i + (b + 1))
                    if b == 0:
                        pe.wait_ge(v_in, 256 * i + 256)
                    if j == 0:
                        after(pe, o_out, 6 * i + max(q - 1, 0))
                    for c in range(nc_):
                        mm = nc.tensor.matmul(pO[q % 2][rows, j * P:(j + 1) * P], vb[:, SEG_RG[s] + c, j, rows],
                                              pt[:, b % 2, c * P:(c + 1) * P], start=(c == 0), stop=(c == nc_ - 1))
                    mm.then_inc(pv_done, 1)

                for slot in range(2 * NCH * len(tiles)):
                    gi, hf = slot // 2, slot % 2
                    n, s = gi % NCH, s_of(i) + gi // NCH
                    bank, _, out = grp(i, gi)
                    if slot < BLK:
                        scores(slot)
                    if hf == 0:
                        if n == 0:
                            pe.wait_ge(w_lo, 8 * i + (s + 1))
                        pe.wait_ge(g_out[bank], out - 1)
                    mm = half_group(bank, s, n, hf)
                    if hf == 1:
                        mm.then_inc(g_done, 1)
                    if 1 <= slot <= BLK:
                        transposes(slot - 1)
                    if 2 <= slot <= BLK + 1:
                        values(slot - 2)

            unit(0)
            with pe.Fori(1, PAIRS - 1) as i:
                unit(i)
            unit(PAIRS - 1)

            def column_sums(of, taken):
                for n in range(NCH):
                    if n == 2:
                        pe.wait_ge(taken, 1)
                    nc.tensor.matmul(pS[n % 2][:], ones, of[:, chunk(n)], start=True, stop=True).then_inc(sum_ps, 1)

            for phase, g0, s0 in ((1, G_YB, S_YB), (2, G_YA, S_YA)):
                for gi in range(24):
                    tile, n = gi // NCH, gi % NCH
                    g, s = g0 + gi, s0 + tile
                    if phase == 1 and gi == 9:
                        pe.wait_ge(csum, KT - 1)
                        pe.wait_ge(ones_ok, 1)
                        column_sums(lnA, mu_ok)
                    if phase == 1 and gi == 15:
                        pe.wait_ge(sq_v, KT - 1)
                        pe.wait_ge(mu_ok, 3)
                        for t in range(NT):
                            mm = nc.tensor.matmul(pS[1][:, t:t + 1], lnA[:, t * P:(t + 1) * P], ones[:, 0:1],
                                                  start=True, stop=True)
                        mm.then_inc(sum_ps, 1)
                    if phase == 1 and gi == 16:
                        pe.wait_ge(diag_ok, 1)
                        column_sums(tmp3, lnr_ok)
                    if n == 0:
                        pe.wait_ge(w_lo, s + 1)
                    pe.wait_ge(g_out[g % 2], g // 2)
                    ready = 24 * phase + KT * n if tile == 0 else None
                    half_group(g % 2, s, n, 0, ready)
                    half_group(g % 2, s, n, 1, ready).then_inc(g_done, 1)
            for e in range(2 * NT):
                token_group(G_OUT + e, S_OUT + 4 * (e // NT), e % NT, 3, e < NT)


def window_masks():
    r, c = np.arange(P) // QB, np.arange(P) % QB
    tiles = []
    for s in range(3):
        rows = np.arange(SEG_ROWS[s])[None, :]
        if s == 0:
            first = np.zeros(P, int)
        elif s == 1:
            first = np.clip(r - 4, 0, 8)
        else:
            first = np.clip(r + 8 - 4, 0, 8) - 4
        row_ok = (rows >= first[:, None]) & (rows < first[:, None] + 8)
        for j in (0, 1, 3):
            key, q = BAND_START[j] + np.arange(BAND)[None, :], (QB * j + c)[:, None]
            w = np.clip(q - 8, 0, GRID - 16)
            col_ok = (key >= w) & (key < w + 16)
            tiles.append(np.where(row_ok[:, :, None] & col_ok[:, None, :], 0.0, BIG).reshape(P, -1))
    return np.concatenate(tiles, 1).astype(np.float32)


INPUTS = ["x_prompt", "x_sample", "norm_g", "w_in", "b_gate", "dw_w", "dw_b", "ln_g", "ln_b", "w_pw_a", "rpb",
          "w_o_b", "w_out", "final_g"]


def kernel(**inputs):
    import concourse.bacc as bacc
    from concourse.bass_utils import run_bass_kernel_spmd

    nc = bacc.Bacc("TRN2", target_bir_lowering=False, num_devices=1)
    arrays, args = {}, []
    for name in INPUTS + ["masks"]:
        a = window_masks() if name == "masks" else np.ascontiguousarray(inputs[name])
        arrays[f"in_{name}"] = a
        args.append(nc.dram_tensor(f"in_{name}", a.shape, mybir.dt.from_np(a.dtype), kind="ExternalInput").ap())
    for name, n in (("y_prompt", PROMPT), ("y_sample", SAMPLE)):
        args.append(nc.dram_tensor(name, (1, n, D), F32, kind="ExternalOutput").ap())
    build(nc, *args)
    r = run_bass_kernel_spmd(nc, [arrays], core_ids=[0]).results[0]
    return r["y_prompt"], r["y_sample"]
```
